# Optimizing a Trainium2 kernel written in Bass

```python
import math
import jax
import jax.numpy as jnp
from jax import lax
import numpy as np

D_MODEL = 2048
BATCH = 1
SEQ = 256
DEPTH = 2
DEC_BATCH = 1
DEC_SEQ = 512
PAST_LEN = 128

HEAD_DIM = 64
N_HEADS_TOTAL = D_MODEL // HEAD_DIM
H_C = N_HEADS_TOTAL // 4
H_A = (N_HEADS_TOTAL - H_C) // 2
H_B = N_HEADS_TOTAL - H_C - H_A
KV_A = H_A // 4
KV_B = H_B // 4
KV_C = H_C // 4
C_PATTERNS = ((128, 1), (512, 4), (2048, 16))
N_C_GROUPS = len(C_PATTERNS)
D_MIX = (H_A + H_B + H_C) * HEAD_DIM
BLOCK = 128
WIN_A = 128
GRID_W = 64
ROPE_THETA = 10000.0
T5_BUCKETS = 32
T5_MAX_DISTANCE = 1024
N_BIAS_HEADS = H_A + N_C_GROUPS * H_C
RMS_EPS = 1e-6
NEG_INF = -1e30
SPLIT_SIZES = (
    H_A * HEAD_DIM, KV_A * HEAD_DIM, KV_A * HEAD_DIM, H_A * HEAD_DIM,
    H_B * HEAD_DIM, KV_B * HEAD_DIM, KV_B * HEAD_DIM, H_B * HEAD_DIM,
    N_C_GROUPS * H_C * HEAD_DIM, N_C_GROUPS * KV_C * HEAD_DIM, N_C_GROUPS * KV_C * HEAD_DIM, H_C * HEAD_DIM,
)
D_IN_PROJ = sum(SPLIT_SIZES)

kernel_name = "hybrid_parallel_group_encoder"

def rms_norm(x, g):
    xf = x.astype(jnp.float32)
    xf = xf * lax.rsqrt(jnp.mean(xf * xf, axis=-1, keepdims=True) + RMS_EPS)
    return xf * g.astype(jnp.float32)

def t5_bucket(rel):
    half = T5_BUCKETS // 2
    max_exact = half // 2
    n = jnp.abs(rel)
    log_ratio = jnp.log(jnp.maximum(n, 1).astype(jnp.float32) / max_exact) / math.log(T5_MAX_DISTANCE / max_exact)
    large = jnp.minimum(max_exact + (log_ratio * (half - max_exact)).astype(jnp.int32), half - 1)
    return jnp.where(rel > 0, half, 0) + jnp.where(n < max_exact, n, large)

def rotate_axis(x, ang):
    n2 = x.shape[-1] // 2
    x1, x2 = x[..., :n2], x[..., n2:]
    c = jnp.cos(ang)[None, :, None, :]
    s = jnp.sin(ang)[None, :, None, :]
    return jnp.concatenate([x1 * c - x2 * s, x1 * s + x2 * c], axis=-1)

def axial_rope(x, ang_row, ang_col):
    half = HEAD_DIM // 2
    return jnp.concatenate([rotate_axis(x[..., :half], ang_row), rotate_axis(x[..., half:], ang_col)], axis=-1)

def window_sink_attention(q, k, v, sink, rel_bias):
    B, S = q.shape[0], q.shape[1]
    nb = S // BLOCK
    R = H_A // KV_A
    span = BLOCK + 2 * WIN_A
    qb = (q * HEAD_DIM ** -0.5).reshape(B, nb, BLOCK, KV_A, R, HEAD_DIM).transpose(1, 0, 2, 3, 4, 5)
    pad = ((0, 0), (WIN_A, WIN_A), (0, 0), (0, 0))
    kp = jnp.pad(k.astype(jnp.float32), pad)
    vp = jnp.pad(v.astype(jnp.float32), pad)
    rel = jnp.arange(span, dtype=jnp.int32)[None, :] - WIN_A - jnp.arange(BLOCK, dtype=jnp.int32)[:, None]
    band = jnp.abs(rel) <= WIN_A
    bias = rel_bias[t5_bucket(rel)][:, :, :H_A]
    bias = bias.transpose(2, 0, 1).reshape(KV_A, R, BLOCK, span).astype(jnp.float32)
    sink_l = sink.astype(jnp.float32).reshape(KV_A, R, 1)

    def one_block(args):
        qblk, start = args
        kb = lax.dynamic_slice_in_dim(kp, start, span, axis=1)
        vb = lax.dynamic_slice_in_dim(vp, start, span, axis=1)
        kpos = start - WIN_A + jnp.arange(span, dtype=jnp.int32)
        mask = band & ((kpos >= 0) & (kpos < S))[None, :]
        s = jnp.einsum('bqhrd,bkhd->bhrqk', qblk, kb) + bias
        s = jnp.where(mask, s, NEG_INF)
        m = jnp.maximum(jnp.max(s, axis=-1), sink_l)
        e = jnp.exp(s - m[..., None])
        denom = jnp.sum(e, axis=-1) + jnp.exp(sink_l - m)
        return jnp.einsum('bhrqk,bkhd->bqhrd', e / denom[..., None], vb)

    starts = jnp.arange(nb, dtype=jnp.int32) * BLOCK
    o = lax.map(one_block, (qb, starts))
    return o.transpose(1, 0, 2, 3, 4, 5).reshape(B, S, H_A * HEAD_DIM)

def global_axial_attention(q, k, v):
    B, S = q.shape[0], q.shape[1]
    nb = S // BLOCK
    R = H_B // KV_B
    qb = (q * HEAD_DIM ** -0.5).reshape(B, nb, BLOCK, KV_B, R, HEAD_DIM).transpose(1, 0, 2, 3, 4, 5)
    kf = k.astype(jnp.float32)
    vf = v.astype(jnp.float32)

    def one_block(qblk):
        s = jnp.einsum('bqhrd,bkhd->bhrqk', qblk, kf)
        p = jax.nn.softmax(s, axis=-1)
        return jnp.einsum('bhrqk,bkhd->bqhrd', p, vf)

    o = lax.map(one_block, qb)
    return o.transpose(1, 0, 2, 3, 4, 5).reshape(B, S, H_B * HEAD_DIM)

def dilated_mixture_attention(q, k, v, rel_bias):
    B, S = q.shape[0], q.shape[1]
    nb = S // BLOCK
    R = H_C // KV_C
    qb = (q * HEAD_DIM ** -0.5).reshape(B, nb, BLOCK, N_C_GROUPS, KV_C, R, HEAD_DIM).transpose(1, 0, 2, 3, 4, 5, 6)
    kf = k.astype(jnp.float32).reshape(B, S, N_C_GROUPS, KV_C, HEAD_DIM)
    vf = v.astype(jnp.float32).reshape(B, S, N_C_GROUPS, KV_C, HEAD_DIM)
    k_groups = [kf[:, :, g] for g in range(N_C_GROUPS)]
    v_groups = [vf[:, :, g] for g in range(N_C_GROUPS)]
    offsets, biases = [], []
    for g, (w, d) in enumerate(C_PATTERNS):
        radius = w // (2 * d)
        off = jnp.arange(-radius, radius + 1, dtype=jnp.int32) * d
        b = rel_bias[t5_bucket(off)][:, H_A + g * H_C: H_A + (g + 1) * H_C]
        biases.append(b.T.reshape(KV_C, R, 1, off.shape[0]).astype(jnp.float32))
        offsets.append(off)

    def one_block(args):
        qblk, start = args
        qpos = start + jnp.arange(BLOCK, dtype=jnp.int32)
        outs, lses = [], []
        for g in range(N_C_GROUPS):
            idx = qpos[:, None] + offsets[g][None, :]
            valid = (idx >= 0) & (idx < S)
            idxc = jnp.clip(idx, 0, S - 1)
            kg = k_groups[g][:, idxc]
            vg = v_groups[g][:, idxc]
            s = jnp.einsum('bqhrd,bqkhd->bhrqk', qblk[:, :, g], kg) + biases[g]
            s = jnp.where(valid[None, None, None], s, NEG_INF)
            lse = jax.nn.logsumexp(s, axis=-1)
            p = jnp.exp(s - lse[..., None])
            outs.append(jnp.einsum('bhrqk,bqkhd->bqhrd', p, vg))
            lses.append(lse)
        alpha = jax.nn.softmax(jnp.stack(lses, axis=0), axis=0).transpose(0, 1, 4, 2, 3)
        return jnp.sum(jnp.stack(outs, axis=0) * alpha[..., None], axis=0)

    starts = jnp.arange(nb, dtype=jnp.int32) * BLOCK
    o = lax.map(one_block, (qb, starts))
    return o.transpose(1, 0, 2, 3, 4, 5).reshape(B, S, H_C * HEAD_DIM)

def trunk(x, ln_g, w_in, q_norm_a, k_norm_a, sink_a, q_norm_b, k_norm_b, q_norm_c, k_norm_c, rel_bias, w_out):
    B, S = x.shape[0], x.shape[1]
    rows = S // GRID_W
    row = jnp.repeat(jnp.arange(rows, dtype=jnp.int32), GRID_W)
    col = jnp.arange(S, dtype=jnp.int32) % GRID_W
    n_freq = HEAD_DIM // 4
    inv_freq = ROPE_THETA ** (-jnp.arange(n_freq, dtype=jnp.float32) / n_freq)
    ang_row = row.astype(jnp.float32)[:, None] * inv_freq[None, :]
    ang_col = col.astype(jnp.float32)[:, None] * inv_freq[None, :]
    points = np.cumsum(SPLIT_SIZES)[:-1].tolist()

    def heads(t):
        return t.reshape(B, S, -1, HEAD_DIM)

    for l in range(DEPTH):
        h = rms_norm(x, ln_g[l]).astype(x.dtype)
        proj = jnp.einsum('bsd,de->bse', h, w_in[l])
        qa, ka, va, ga, qb, kb, vb, gb, qc, kc, vc, gc = jnp.split(proj, points, axis=-1)
        ya = window_sink_attention(rms_norm(heads(qa), q_norm_a[l]), rms_norm(heads(ka), k_norm_a[l]),
                                   heads(va), sink_a[l], rel_bias)
        yb = global_axial_attention(axial_rope(rms_norm(heads(qb), q_norm_b[l]), ang_row, ang_col),
                                    axial_rope(rms_norm(heads(kb), k_norm_b[l]), ang_row, ang_col),
                                    heads(vb))
        yc = dilated_mixture_attention(rms_norm(heads(qc), q_norm_c[l]), rms_norm(heads(kc), k_norm_c[l]),
                                       heads(vc), rel_bias)
        mix = jnp.concatenate([ya * jax.nn.silu(ga.astype(jnp.float32)),
                               yb * jax.nn.silu(gb.astype(jnp.float32)),
                               yc * jax.nn.silu(gc.astype(jnp.float32))], axis=-1).astype(x.dtype)
        x = x + jnp.einsum('bse,ed->bsd', mix, w_out[l]).astype(x.dtype)
    return x

def setup_inputs(seed: int = 0) -> dict:
    key = jax.random.key(seed)
    ks = jax.random.split(key, 13)
    f32 = jnp.float32
    return {
        "x_prompt": jax.random.normal(ks[0], (BATCH, SEQ, D_MODEL), f32),
        "x_sample": jax.random.normal(ks[1], (DEC_BATCH, DEC_SEQ, D_MODEL), f32),
        "ln_g": 1.0 + 0.05 * jax.random.normal(ks[2], (DEPTH, D_MODEL), f32),
        "w_in": jax.random.normal(ks[3], (DEPTH, D_MODEL, D_IN_PROJ), f32) * D_MODEL ** -0.5,
        "q_norm_a": 1.0 + 0.05 * jax.random.normal(ks[4], (DEPTH, HEAD_DIM), f32),
        "k_norm_a": 1.0 + 0.05 * jax.random.normal(ks[5], (DEPTH, HEAD_DIM), f32),
        "sink_a": 0.5 * jax.random.normal(ks[6], (DEPTH, H_A), f32),
        "q_norm_b": 1.0 + 0.05 * jax.random.normal(ks[7], (DEPTH, HEAD_DIM), f32),
        "k_norm_b": 1.0 + 0.05 * jax.random.normal(ks[8], (DEPTH, HEAD_DIM), f32),
        "q_norm_c": 1.0 + 0.05 * jax.random.normal(ks[9], (DEPTH, HEAD_DIM), f32),
        "k_norm_c": 1.0 + 0.05 * jax.random.normal(ks[10], (DEPTH, HEAD_DIM), f32),
        "rel_bias": 0.1 * jax.random.normal(ks[11], (T5_BUCKETS, N_BIAS_HEADS), f32),
        "w_out": jax.random.normal(ks[12], (DEPTH, D_MIX, D_MODEL), f32) * D_MIX ** -0.5,
    }

def reference(x_prompt, x_sample, ln_g, w_in, q_norm_a, k_norm_a, sink_a, q_norm_b, k_norm_b,
              q_norm_c, k_norm_c, rel_bias, w_out):
    y_prompt = trunk(x_prompt, ln_g, w_in, q_norm_a, k_norm_a, sink_a, q_norm_b, k_norm_b,
                     q_norm_c, k_norm_c, rel_bias, w_out)
    y_sample = trunk(x_sample, ln_g, w_in, q_norm_a, k_norm_a, sink_a, q_norm_b, k_norm_b,
                     q_norm_c, k_norm_c, rel_bias, w_out)
    return (y_prompt, y_sample)


_drawn_inputs = setup_inputs


def setup_inputs(seed=0):
    import zlib

    import numpy as np

    out = dict(_drawn_inputs(seed))
    spreads = {}
    factors = {'ln_g': 6.004,
     'q_norm_a': 8.0,
     'k_norm_a': 8.0,
     'sink_a': 8.0,
     'q_norm_b': 8.0,
     'k_norm_b': 8.0,
     'q_norm_c': 8.0,
     'k_norm_c': 8.0,
     'rel_bias': 8.0}
    for name, (base, spread) in spreads.items():
        noise = np.random.default_rng([zlib.crc32(name.encode()), seed]).standard_normal(out[name].shape)
        drawn = base * np.exp(spread * noise) if base else spread * noise
        out[name] = jnp.asarray(drawn.astype(out[name].dtype))
    for name, factor in factors.items():
        out[name] = (out[name] * factor).astype(out[name].dtype)
    return out
```

```python
import math
from contextlib import ExitStack

import numpy as np

import concourse.bass as bass
from concourse import mybir

F32 = mybir.dt.float32
F32R = mybir.dt.float32r
ALU = mybir.AluOpType
ACT = mybir.ActivationFunctionType
AX_X = mybir.AxisListType.X

P = 128
D = 2048
DEPTH = 2
SEQS = (256, 512)
TOKENS = sum(SEQS)
TT = TOKENS // P
SEQ_TILES = ((0, 2), (2, 6))
DH = 64
H_A, H_B, H_C = 12, 12, 8
KV_A, KV_B, KV_C = 3, 3, 2
NG_C = 3
C_PATTERNS = ((128, 1), (512, 4), (2048, 16))
WIN_A = 128
GRID_W = 64
N_FREQ = DH // 4
BUCKETS = 32
N_BIAS = H_A + NG_C * H_C
EPS = 1e-6
MASKED = 1e30

UNIT_RUNS = (("q", "A", H_A), ("k", "A", KV_A), ("v", "A", KV_A), ("g", "A", H_A),
             ("q", "B", H_B), ("k", "B", KV_B), ("v", "B", KV_B), ("g", "B", H_B),
             ("q", "C", NG_C * H_C), ("k", "C", NG_C * KV_C), ("v", "C", NG_C * KV_C), ("g", "C", H_C))
UNITS = [(kind, mixer) for kind, mixer, n in UNIT_RUNS for _ in range(n)]
E = len(UNITS) * DH
KC = D // P
SLAB = 512
UPS = SLAB // DH
NS_IN = E // SLAB
NS_OUT = D // SLAB
CHUNKS_IN = NS_IN * KC
CHUNKS_OUT = NS_OUT * KC
CHUNKS = CHUNKS_IN + CHUNKS_OUT
GAIN = {("q", "A"): 0, ("k", "A"): 1, ("q", "B"): 2, ("k", "B"): 3, ("q", "C"): 4, ("k", "C"): 5}


def index_units():
    blocks = vs = gs = 0
    at = []
    for kind, _ in UNITS:
        if kind in "qk":
            at.append(blocks)
            blocks += 1
        elif kind == "v":
            at.append(vs)
            vs += 1
        else:
            at.append(gs)
            gs += 1
    return at, blocks, vs, gs


PLACE, BLOCKS, VHEADS, GHEADS = index_units()


U_QC, U_KC, U_VC, U_GC = 60, 84, 90, 96
assert UNITS[U_QC][0] == "q" and UNITS[U_KC] == ("k", "C") and UNITS[U_VC] == ("v", "C") and UNITS[U_GC] == ("g", "C")
SLAB_UNITS = [list(range(UPS * s, UPS * (s + 1))) for s in range(7)] + [
    [*range(56, 60), U_KC, U_KC + 1, U_VC, U_VC + 1],
    *[list(range(U_QC + g * H_C, U_QC + (g + 1) * H_C)) for g in range(NG_C)],
    [U_VC + 2, U_VC + 3, *range(U_KC + 2, U_KC + 6), U_VC + 4, U_VC + 5],
    list(range(U_GC, U_GC + UPS))]
assert sorted(u for units in SLAB_UNITS for u in units) == list(range(len(UNITS)))
INTERLEAVED = [9, 10, 11]



def runs_of(slab):
    runs = []
    for i, unit in enumerate(SLAB_UNITS[slab]):
        kind, mixer = UNITS[unit]
        if runs and runs[-1][:2] == (kind, mixer):
            runs[-1] = (kind, mixer, runs[-1][2], runs[-1][3] + 1)
        else:
            runs.append((kind, mixer, i, 1))
    return runs


def pieces_of(slab):
    pieces = []
    for i, unit in enumerate(SLAB_UNITS[slab]):
        if pieces and pieces[-1][0] + pieces[-1][2] == unit * DH:
            pieces[-1] = (pieces[-1][0], pieces[-1][1], pieces[-1][2] + DH)
        else:
            pieces.append((unit * DH, i * DH, DH))
    return pieces


def token_order(tile, interleaved):
    lo, hi = next(x for x in SEQ_TILES if x[0] <= tile < x[1])
    return (lo * P + tile - lo, hi - lo) if interleaved else (tile * P, 1)


assert all(d % (hi - lo) == 0 for _, d in C_PATTERNS[1:] for lo, hi in SEQ_TILES)
RUNS = [runs_of(s) for s in range(NS_IN)]
HEAD_RUNS = [[r for r in RUNS[s] if r[0] in "qk"] for s in range(NS_IN)]
GATE_RUNS = [[r for r in RUNS[s] if r[0] == "g"] for s in range(NS_IN)]
V_RUNS = [[r for r in RUNS[s] if r[0] == "v"] for s in range(NS_IN)]
SLAB_BLOCKS = [sum(r[3] for r in HEAD_RUNS[s]) for s in range(NS_IN)]
MAX_BLOCKS = max(SLAB_BLOCKS)

TABLE_W = (1, 1, 0, 0, 0, 0)
TABLE_REACH = [(WIN_A, 1, 1), (C_PATTERNS[0][0] // 2, 1, 1)] + [
    (w // 2, hi - lo, d) for w, d in C_PATTERNS[1:] for lo, hi in SEQ_TILES]
TABLE_COLS = [(2 * w + 1) * P for w in TABLE_W]
ROW_LEN = [c + P - 1 for c in TABLE_COLS]
ROW_AT = [sum(ROW_LEN[:i]) for i in range(len(TABLE_W))]
ROWS_ALL = sum(ROW_LEN)
BIAS_COLS = 4 * TABLE_COLS[0]


def t5_bucket(rel):
    half = BUCKETS // 2
    exact = half // 2
    n = np.abs(rel)
    ratio = np.log(np.maximum(n, 1).astype(np.float32) / np.float32(exact)) / np.float32(math.log(1024 / exact))
    large = np.minimum(exact + (ratio * (half - exact)).astype(np.int32), half - 1)
    return np.where(rel > 0, half, 0) + np.where(n < exact, n, large)


def bias_selector():
    sel = np.zeros((BUCKETS + 1, ROWS_ALL), np.float32)
    for kind, (radius, step, dilation) in enumerate(TABLE_REACH):
        tokens = ((TABLE_W[kind] + 1) * P - 1 - np.arange(ROW_LEN[kind])) * step
        seen = (np.abs(tokens) <= radius) & (tokens % dilation == 0)
        cols = ROW_AT[kind] + np.arange(ROW_LEN[kind])
        sel[t5_bucket(tokens)[seen], cols[seen]] = -1.0
        sel[BUCKETS, cols[~seen]] = MASKED
    return sel


def rope_table():
    pos = np.arange(max(SEQS)).reshape(-1, P).T
    inv = np.float32(10000.0) ** (-np.arange(N_FREQ, dtype=np.float32) / np.float32(N_FREQ))
    row = (pos // GRID_W).astype(np.float32)[:, :, None] * inv
    col = (pos % GRID_W).astype(np.float32)[:, :, None] * inv
    cos = np.concatenate([np.cos(row), np.cos(row), np.cos(col), np.cos(col)], -1)
    sin = np.concatenate([-np.sin(row), np.sin(row), -np.sin(col), np.sin(col)], -1)
    return np.ascontiguousarray(np.stack([cos, sin], 2).astype(np.float32))


def attention_units():
    first = {}
    for i, unit in enumerate(UNITS):
        first.setdefault(unit, i)

    def unit(kind, mixer, j, g, table, reach, bias_head):
        heads, kvs = (H_C, KV_C) if mixer == "C" else (0, 0)
        return dict(kind=kind, q=PLACE[first["q", mixer] + g * heads + 4 * j], k=PLACE[first["k", mixer] + g * kvs + j],
                    v=PLACE[first["v", mixer] + g * kvs + j], j=j, g=g, table=table, reach=reach, bias_head=bias_head,
                    gate={"A": 0, "B": H_A, "C": H_A + H_B}[mixer] // 2 + 2 * j)

    a = [unit("A", "A", j, 0, 0, 1, 4 * j) for j in range(KV_A)]
    quads = [unit("Q", "C", j, g, 2 * g, 0, H_A + g * H_C + 4 * j) for j in range(KV_C) for g in (1, 2)]
    c = [unit("C", "C", j, 0, 1, 1, H_A + 4 * j) for j in range(KV_C)]
    b = [unit("B", "B", j, 0, None, 3, 0) for j in range(KV_B)]
    return a[:-1] + quads + a[-1:] + c, b


OTHERS, B_UNITS = attention_units()
ATT_UNITS = OTHERS + B_UNITS
PART = 2 * DH + 4


def unit_items(u):
    return [(u, hp, t) for hp in ((None,) if ATT_UNITS[u]["kind"] == "Q" else (0, 1)) for t in range(TT)]


def attention_items():
    others = [x for u in range(len(OTHERS)) for x in unit_items(u)]
    each = len(others) // len(B_UNITS)
    order = []
    for j in range(len(B_UNITS)):
        zone, mine = others[j * each:(j + 1) * each], unit_items(len(OTHERS) + j)
        spread = len(zone) - B_REST
        for i, item in enumerate(zone):
            order.append(item)
            while mine and len(mine) > len(unit_items(len(OTHERS) + j)) * (1 - (i + 1) / spread) + 1e-9:
                order.append(mine.pop(0))
        assert not mine
    items, steps = [], []
    for u, hp, t in order:
        unit = ATT_UNITS[u]
        lo, hi = next(x for x in SEQ_TILES if x[0] <= t < x[1])
        a, b = max(lo, t - unit["reach"]), min(hi, t + unit["reach"] + 1)
        for r in (None,) if hp is None else (0, 1):
            steps.append(dict(item=len(items), u=u, unit=unit, kind=unit["kind"], hp=hp, t=t, r=r, a=a, b=b,
                              tiles=4 if r is None else b - a, last=r != 0))
        items.append(dict(u=u, unit=unit, kind=unit["kind"], hp=hp, t=t, step=len(steps) - 1))
    return items, steps


B_REST = 7
ITEMS, STEPS = attention_items()
N_ITEMS, N_STEPS = len(ITEMS), len(STEPS)
for _kinds, _name in (("ABC", "pair_no"), ("Q", "quad_no"), ("C", "merge_no")):
    for _n, _it in enumerate([x for x in ITEMS if x["kind"] in _kinds]):
        _it[_name] = _n
N_PAIRS = sum(x["kind"] in "ABC" for x in ITEMS)
N_QUADS = sum(x["kind"] == "Q" for x in ITEMS)
N_MERGES = sum(x["kind"] == "C" for x in ITEMS)
SUNK = np.cumsum([x["kind"] == "A" for x in STEPS]).tolist()
UNIT_FIRST = [min(i for i, it in enumerate(ITEMS) if it["u"] == u) for u in range(len(ATT_UNITS))]
UNIT_END = [max(i for i, it in enumerate(ITEMS) if it["u"] == u) for u in range(len(ATT_UNITS))]
LOAD_AT = {}
for _u in range(1, len(OTHERS)):
    LOAD_AT.setdefault(UNIT_FIRST[_u] - 1, []).append(_u)
for _u in range(len(OTHERS) + 1, len(ATT_UNITS)):
    LOAD_AT.setdefault(UNIT_END[_u - 1] + 6, []).append(_u)
BIAS_UNITS = [u for u, x in enumerate(ATT_UNITS) if x["kind"] != "B"]
BIAS_NO = {u: i for i, u in enumerate(BIAS_UNITS)}
UNIT_LAST = [max(i for i, st in enumerate(STEPS) if st["u"] == u) for u in range(len(ATT_UNITS))]
S_BANKS = 3
P_SLOTS = 6
P_COLS = 4 * P + 8
PT_BANKS = 2
PT_SLOTS = 5
Q_SLOTS = 4
GATE_SLOTS = 7
KV_SLOTS = 3
PART_SLOTS = 8
MERGE_SLOTS = 4
STAT_SLOTS = 8
MIN_LAG = 1
MERGE_LAG = 1
T_LAG = 3
V_LAG = 4
MIX_LAG = 5
X_LAG = 7
LO_LAG = 8


def on_act(step):
    return step % 2 == 1


ACT_COPIES = np.cumsum([on_act(i) for i in range(N_STEPS)]).tolist()

W_RAW = 3
W_RING = 6
LEAD = 4
NORM_LEAD = 2
SQUARE_SLOTS = [2, 5, 8, 11]
NORM_EARLY = KC - KC // NS_OUT
PER_LOAD = 4
RAW_SLOTS = TT


def post_schedule():
    work = {}
    for s in range(NS_IN):
        for t in range(TT):
            base = KC * (s + 1)
            at = base + (t if s == NS_IN - 2 else 2 * t)
            for step, slot in (("drain", base), ("sums", at), ("scale", at + 1), ("rope", at + 2), ("split", at + 3),
                               ("turn", at + 5), ("store", at + 6)):
                work.setdefault(slot, []).append((step, s, t))
    return work


POST = post_schedule()
HEAD_TILES = [(l, s, t) for l in range(DEPTH) for s in range(NS_IN) if HEAD_RUNS[s] for t in range(TT)]
GATE_TILES = [(l, s, t) for l in range(DEPTH) for s in range(NS_IN) if GATE_RUNS[s] for t in range(TT)]
ROPE_TILES = [(l, s, t) for l, s, t in HEAD_TILES if any(r[1] == "B" for r in HEAD_RUNS[s])]
HEAD_AT = {x: i for i, x in enumerate(HEAD_TILES)}
GATE_AT = {x: i for i, x in enumerate(GATE_TILES)}
ROPE_AT = {x: i for i, x in enumerate(ROPE_TILES)}


NORM_TILES = TT // 2
NORM_GROUPS = 2


def turn_groups():
    order = []
    for l in range(DEPTH):
        order += [(l, "norm", k, g, NORM_TILES) for k in range(KC) for g in range(NORM_GROUPS)]
        for slot in sorted(POST):
            for step, s, t in POST[slot]:
                if step == "turn":
                    order += [(l, s, t, b, min(4, SLAB_BLOCKS[s] - b)) for b in range(0, SLAB_BLOCKS[s], 4)]
    return order


TURNS = turn_groups()
TURN_AT = {x[:4]: i for i, x in enumerate(TURNS)}
TURN_BANKS = 2


def turn_on_act(i):
    return i % 2 == 0


TURN_ACT = np.cumsum([x[1] != "norm" and turn_on_act(i) for i, x in enumerate(TURNS)]).tolist()
TURN_DVE = np.cumsum([x[1] != "norm" and not turn_on_act(i) for i, x in enumerate(TURNS)]).tolist()
NORM_AT = {x[:4]: i for i, x in enumerate([y for y in TURNS if y[1] == "norm"])}


def build(nc, x_prompt, x_sample, ln_g, w_in, q_norm_a, k_norm_a, sink_a, q_norm_b, k_norm_b,
          q_norm_c, k_norm_c, rel_bias, w_out, selector, rope, identity, y_prompt, y_sample):
    with ExitStack() as ctx:
        def dram(name, shape):
            return nc.dram_tensor(name, shape, F32, kind="Internal").ap()

        def sem(name):
            return ctx.enter_context(nc.semaphore(name))

        heads_t = dram("heads_t", [TT, P, BLOCKS * P])
        v_rows = dram("v_rows", [TOKENS, VHEADS * DH])
        gate_rows = dram("gate_rows", [TOKENS, GHEADS * DH])
        x_mid = dram("x_mid", [TOKENS, D])
        rstd_rows = dram("rstd_rows", [TOKENS])
        bias_rows = dram("bias_rows", [N_BIAS, ROWS_ALL])
        part_rows = dram("part_rows", [TOKENS, 2, KV_C, 2, PART])

        top = [nc.sbuf_base]

        def sb(name, shape, dtype=F32):
            size = 4 * int(np.prod(shape[1:]))
            at = (top[0] + 31) // 32 * 32
            top[0] = at + size
            return nc.alloc_sbuf_tensor_at(name, shape, dtype, offset=at)

        first = top[0]
        act_hi = sb("act_hi", [P, KC, TOKENS], F32R)
        act_lo = sb("act_lo", [P, KC, TOKENS], F32R)
        after = top[0]
        top[0] = first + 4 * TOKENS * (KC // 2)
        sel_sb = sb("sel_sb", [BUCKETS + 1, ROWS_ALL])
        rb_sb = sb("rb_sb", [BUCKETS + 1, N_BIAS])
        assert top[0] <= first + 4 * TOKENS * KC
        top[0] = first + 4 * TOKENS * (KC + KC // 2)
        rows_sb = sb("rows_sb", [N_BIAS, ROWS_ALL])
        assert top[0] <= after
        top[0] = after
        ident = sb("ident", [P, P])
        sinks = sb("sinks", [P, DEPTH * H_A])
        half = sb("half", [P, UPS])
        minus_one = sb("minus_one", [P, 2])
        ln_rows = sb("ln_rows", [DEPTH * KC, P])
        ln_cols = sb("ln_cols", [P, DEPTH * KC])
        x_sums = sb("x_sums", [P, TT, NS_OUT])
        x_stat = sb("x_stat", [P, 2, TT])
        w_raw = sb("w_raw", [P, W_RAW, PER_LOAD, SLAB])
        overlay = top[0]
        w_hi = sb("w_hi", [P, W_RING, SLAB], F32R)
        w_lo = sb("w_lo", [P, W_RING, SLAB], F32R)
        rope_t = sb("rope_t", [P, max(SEQS) // P, 2, DH])
        gains = sb("gains", [P, 6, DH])
        stats = sb("stats", [P, TT, UPS])
        work = top[0]
        x_cols = sb("x_cols", [P, NS_OUT, TT, SLAB])
        junk = sb("junk", [P, 2, SLAB])
        ends = [top[0]]
        top[0] = work
        y = sb("y", [P, 2, SLAB])
        sq = sb("sq", [P, 2, SLAB])
        rot = sb("rot", [P, 2, SLAB])
        pairs = sb("pairs", [P, 2, MAX_BLOCKS, P], F32R)
        turned = sb("turned", [P, 2, MAX_BLOCKS, P])
        ends.append(top[0])
        top[0] = work
        q_t = sb("q_t", [P, Q_SLOTS, 4, P], F32R)
        k_t = sb("k_t", [P, KV_SLOTS, TT, 2, P], F32R)
        v_t = sb("v_t", [P, KV_SLOTS, TT, DH])
        bias0 = sb("bias0", [P, BIAS_COLS])
        bias1 = sb("bias1", [P, BIAS_COLS])
        late = max(top[0], ends[1])
        top[0] = overlay
        prob = sb("prob", [P, P_SLOTS, P_COLS])
        prob_t = sb("prob_t", [P, PT_SLOTS, 4 * P])
        gate = sb("gate", [P, GATE_SLOTS, P])
        mix = sb("mix", [P, 2, P])
        minus_max = sb("minus_max", [P, STAT_SLOTS, 2])
        denom = sb("denom", [P, STAT_SLOTS, 2])
        recip = sb("recip", [P, 2, 2])
        assert top[0] <= work, (top[0], work)
        bias = (bias0, bias1)
        top[0] = late
        raw = sb("raw", [P, RAW_SLOTS, SLAB])
        ends.append(top[0])
        top[0] = late
        part_out = sb("part_out", [P, PART_SLOTS, 2, PART])
        part_in = sb("part_in", [P, MERGE_SLOTS, 2, PART])
        part_sum = sb("part_sum", [P, 2, 2, P])
        merge_min = sb("merge_min", [P, MERGE_SLOTS, 2])
        merge_w = sb("merge_w", [P, MERGE_SLOTS, 3, 2])
        merge_d = sb("merge_d", [P, MERGE_SLOTS, 3, 2])
        ends.append(top[0])
        assert max(ends) <= nc.sbuf_usable_end, (ends, nc.sbuf_usable_end)

        bank = [ctx.enter_context(nc.psum_tensor(f"bank{i}", [P, SLAB], F32)) for i in range(8)]
        acc = bank[0:6]
        turn_bank = bank[6:8]
        s_bank = bank[0:3]
        pt_bank = bank[3:5]
        o_bank = bank[5:7]
        mix_bank = bank[7]

        ident_loaded = sem("ident_loaded")
        set_loaded = sem("set_loaded")
        set_dve = sem("set_dve")
        rows_done = sem("rows_done")
        rows_copied = sem("rows_copied")
        rows_stored = sem("rows_stored")
        w_loaded = [sem(f"w_loaded{i}") for i in range(W_RAW)]
        w_hi_done = sem("w_hi_done")
        w_lo_done = sem("w_lo_done")
        w_used = sem("w_used")
        x_loaded = [sem(f"x_loaded{i}") for i in range(NS_OUT)]
        ln_loaded = sem("ln_loaded")
        ln_turned = sem("ln_turned")
        ln_copied = sem("ln_copied")
        rope_loaded = sem("rope_loaded")
        gains_loaded = sem("gains_loaded")
        gains_scaled = sem("gains_scaled")
        x_squared = sem("x_squared")
        x_chain = sem("x_chain")
        x_rstd_stored = sem("x_rstd_stored")
        x_rstd_back = sem("x_rstd_back")
        turn_done = sem("turn_done")
        norm_hi = sem("norm_hi")
        norm_lo = sem("norm_lo")
        turn_act = sem("turn_act")
        turn_dve = sem("turn_dve")
        acc_done = sem("acc_done")
        acc_copied = sem("acc_copied")
        acc_added = sem("acc_added")
        squared = sem("squared")
        summed = sem("summed")
        rstd_chain = sem("rstd_chain")
        rstd_done = sem("rstd_done")
        scaled = sem("scaled")
        gained = sem("gained")
        roped = sem("roped")
        hi_split = sem("hi_split")
        lo_split = sem("lo_split")
        heads_stored = [sem(f"heads_stored{i}") for i in range(2)]
        gates_stored = sem("gates_stored")
        v_stored = sem("v_stored")
        q_loaded = [sem(f"q_loaded{i}") for i in range(Q_SLOTS)]
        gate_loaded = [sem(f"gate_loaded{i}") for i in range(GATE_SLOTS)]
        kv_loaded = [sem(f"kv_loaded{i}") for i in range(KV_SLOTS)]
        bias_loaded = [sem(f"bias_loaded{i}") for i in range(2)]
        part_loaded = [sem(f"part_loaded{i}") for i in range(MERGE_SLOTS)]
        part_stored = [sem(f"part_stored{i}") for i in range(PART_SLOTS)]
        scored = sem("scored")
        biased = sem("biased")
        sunk = sem("sunk")
        exped = sem("exped")
        p_turned = sem("p_turned")
        pt_act = sem("pt_act")
        pt_dve = sem("pt_dve")
        pv_done = sem("pv_done")
        part_taken = sem("part_taken")
        merge_mins = sem("merge_mins")
        merge_args = sem("merge_args")
        merge_exps = sem("merge_exps")
        merge_chain = sem("merge_chain")
        recips = sem("recips")
        mixed = sem("mixed")
        mix_turned = sem("mix_turned")
        mix_hi = sem("mix_hi")
        mix_lo = sem("mix_lo")
        x_stored = sem("x_stored")

        def prob_copied(eng, l, i):
            n_act = l * ACT_COPIES[-1] + ACT_COPIES[i]
            eng.wait_ge(pt_act if on_act(i) else pt_dve, n_act if on_act(i) else l * N_STEPS + i + 1 - n_act)

        def turn_evacuated(eng, i):
            l, s, t, b, _ = TURNS[i]
            if s == "norm":
                eng.wait_ge(norm_lo, NORM_AT[l, s, t, b] + 1)
            elif turn_on_act(i):
                eng.wait_ge(turn_act, TURN_ACT[i])
            else:
                eng.wait_ge(turn_dve, TURN_DVE[i])

        def kv_place(l, u):
            if u >= len(OTHERS):
                return KV_SLOTS - 1, l * len(B_UNITS) + u - len(OTHERS) + 1
            n = l * len(OTHERS) + u
            return n % (KV_SLOTS - 1), n // (KV_SLOTS - 1) + 1

        def bias_in(eng, l, b):
            each_layer = (len(BIAS_UNITS) + 1 - b % 2) // 2
            eng.wait_ge(bias_loaded[b % 2], 16 * 4 * (l * each_layer + b // 2 + 1))

        def x_slab(l, s, last):
            cols = slice(s * SLAB, (s + 1) * SLAB)
            if last:
                l += 1
            if 0 < l < DEPTH:
                return [x_mid[lo * P:hi * P, cols] for lo, hi in SEQ_TILES]
            ends_of_x = (y_prompt, y_sample) if l == DEPTH else (x_prompt, x_sample)
            return [x[0, :, cols] for x in ends_of_x]

        def weight_pieces(l, load):
            s, q = divmod(load, KC // PER_LOAD)
            rows = slice(q * PER_LOAD * P, (q + 1) * PER_LOAD * P)
            if s < NS_IN:
                return [(w_in[l, rows, c:c + n].rearrange("(j p) n -> p j n", p=P), slice(at, at + n))
                        for c, at, n in pieces_of(s)]
            return [(w_out[l, rows, (s - NS_IN) * SLAB:(s - NS_IN + 1) * SLAB].rearrange("(j p) n -> p j n", p=P),
                     slice(0, SLAB))]

        LOADS = CHUNKS // PER_LOAD
        LOADS_IN = CHUNKS_IN // PER_LOAD

        def heads_before(l):
            return sum(1 for x in HEAD_TILES if x[0] < l)

        def chunk_used(eng, n):
            l, c = divmod(n, CHUNKS)
            s, k = divmod(c, KC)
            if k == KC - 1:
                eng.wait_ge(acc_done, (l * (NS_IN + NS_OUT) + s + 1) * TT)
            else:
                eng.wait_ge(w_used, n + 1 - n // KC)

        def tokens_of(tensor, k, t, interleaved):
            first, step = token_order(t, interleaved)
            return tensor[:, k, first:first + step * (P - 1) + 1:step]

        def ends_pair(i):
            return 0 <= i < N_STEPS and STEPS[i]["last"] and STEPS[i]["kind"] != "Q"

        def ends_quad(i):
            return 0 <= i < N_STEPS and STEPS[i]["kind"] == "Q"

        def ends_merge(i):
            return ends_pair(i) and STEPS[i]["kind"] == "C"

        def v_stores_through(l, s, t):
            return sum(len(V_RUNS[ss]) for ll in range(l + 1) for ss in range(NS_IN) for tt in range(TT)
                       if V_RUNS[ss] and (ll, ss, tt) <= (l, s, t))

        def run_cols(run):
            return run[2] * DH, (run[2] + run[3]) * DH

        def head_cols(s):
            return HEAD_RUNS[s][0][2] * DH, (HEAD_RUNS[s][-1][2] + HEAD_RUNS[s][-1][3]) * DH

        def drain_parts(s):
            parts = []
            for kind, _, u, n in RUNS[s]:
                func = ACT.Silu if kind == "g" else ACT.Copy
                if parts and parts[-1][0] == func:
                    parts[-1] = (func, parts[-1][1], (u + n) * DH)
                else:
                    parts.append((func, u * DH, (u + n) * DH))
            return parts

        def rotated_ready(eng, l, s, t):
            if (l, s, t) in ROPE_AT:
                eng.wait_ge(roped, 5 * ROPE_AT[l, s, t] + 5)
            eng.wait_ge(gained, HEAD_AT[l, s, t] + 1)

        def block_views(s, n):
            a, b = head_cols(s)
            blk = pairs[:, n % 2, 0:SLAB_BLOCKS[s], :]
            return y[:, n % 2, a:b].rearrange("p (h d) -> p h d", d=DH), blk[:, :, 0:DH], blk[:, :, DH:P]

        def copy_turned(eng, copy, i, n, s, b):
            eng.wait_ge(turn_done, i + 1)
            if n >= 2:
                eng.wait_ge(heads_stored[n % 2], 16 * (n // 2))
            nb = min(4, SLAB_BLOCKS[s] - b)
            return copy(turned[:, n % 2, b:b + nb, :].rearrange("p b c -> p (b c)"), turn_bank[i % TURN_BANKS][:, 0:nb * P])

        def copy_pt(eng, copy, l, i):
            n = l * N_STEPS + i
            eng.wait_ge(p_turned, n + 1)
            if i >= PT_SLOTS:
                eng.wait_ge(pv_done, n - PT_SLOTS + 1)
            w = STEPS[i]["tiles"] * P
            return copy(prob_t[:, n % PT_SLOTS, 0:w], pt_bank[n % PT_BANKS][:, 0:w])

        def gates_in_dram(eng, tiles):
            eng.wait_ge(gates_stored, 16 * tiles)

        def heads_in_dram(eng, l):
            for i in range(2):
                eng.wait_ge(heads_stored[i], 16 * ((heads_before(l + 1) + 1 - i) // 2))
            eng.wait_ge(v_stored, 16 * V_STORES * (l + 1))

        block = ctx.enter_context(nc.Block())

        @block.sync
        def _(sp):
            sp.dma_start(ident[:], identity).then_inc(ident_loaded, 16)

            def load_setup():
                sp.dma_start(sel_sb[:], selector).then_inc(set_loaded, 16)
                sp.dma_start(rb_sb[0:BUCKETS, :], rel_bias).then_inc(set_loaded, 16)
                sp.dma_start(sinks[:], sink_a.rearrange("l h -> (l h)").partition_broadcast(P)).then_inc(set_loaded, 16)

            def load_weights(l, m):
                n = l * LOADS + m
                if n >= W_RAW:
                    sp.wait_ge(w_lo_done, PER_LOAD * (n - W_RAW) + PER_LOAD)
                for src, cols in weight_pieces(l, m):
                    sp.dma_start(w_raw[:, n % W_RAW, :, cols], src).then_inc(w_loaded[n % W_RAW], 16)

            def store_gate(l, s, t):
                sp.wait_ge(acc_copied, (l * NS_IN + s) * TT + t + 1)
                (_, _, u, n), = GATE_RUNS[s]
                g0 = PLACE[SLAB_UNITS[s][u]]
                sp.dma_start(gate_rows[t * P:(t + 1) * P, g0 * DH:(g0 + n) * DH],
                             raw[:, t, u * DH:(u + n) * DH]).then_inc(gates_stored, 16)

            def stores(l, slot):
                for step, s, t in POST.get(slot, ()):
                    rows = slice(t * P, (t + 1) * P)
                    if step == "sums" and V_RUNS[s]:
                        sp.wait_ge(acc_copied, (l * NS_IN + s) * TT + t + 1)
                        for _, _, u, n in V_RUNS[s]:
                            v0 = PLACE[SLAB_UNITS[s][u]]
                            sp.dma_start(v_rows[rows, v0 * DH:(v0 + n) * DH],
                                         raw[:, t, u * DH:(u + n) * DH]).then_inc(v_stored, 16)
                    if step == "sums" and s < NS_IN - 1 and GATE_RUNS[s]:
                        store_gate(l, s, t)
                    if step == "store" and HEAD_RUNS[s]:
                        i = HEAD_AT[l, s, t]
                        last = TURN_AT[l, s, t, (SLAB_BLOCKS[s] - 1) // 4 * 4]
                        sp.wait_ge(turn_act, TURN_ACT[last])
                        sp.wait_ge(turn_dve, TURN_DVE[last])
                        b0, nb = PLACE[SLAB_UNITS[s][HEAD_RUNS[s][0][2]]], SLAB_BLOCKS[s]
                        sp.dma_start(heads_t[t, :, b0 * P:(b0 + nb) * P],
                                     turned[:, i % 2, 0:nb, :].rearrange("p b c -> p (b c)"))\
                            .then_inc(heads_stored[i % 2], 16)

            def load_unit(l, u):
                unit = ATT_UNITS[u]
                slot, _ = kv_place(l, u)
                former = u - 1 if u > len(OTHERS) else u - KV_SLOTS + 1 if u < len(OTHERS) else -1
                if former >= 0:
                    sp.wait_ge(pv_done, l * N_STEPS + UNIT_LAST[former] + 1)
                elif l > 0:
                    sp.wait_ge(pv_done, l * N_STEPS)
                for part in range(2):
                    src = heads_t[:, part * DH:(part + 1) * DH, unit["k"] * P:(unit["k"] + 1) * P].rearrange("t p n -> p t n")
                    for to in range(2):
                        sp.dma_start(k_t[to * DH:(to + 1) * DH, slot, :, part, :].bitcast(F32), src)\
                            .then_inc(kv_loaded[slot], 16)
                sp.dma_start(v_t[:, slot, :, :],
                             v_rows[:, unit["v"] * DH:(unit["v"] + 1) * DH].rearrange("(t p) n -> p t n", p=P))\
                    .then_inc(kv_loaded[slot], 16)
                if u in BIAS_NO:
                    b = BIAS_NO[u]
                    if b >= 2:
                        sp.wait_ge(biased, l * N_STEPS + UNIT_LAST[BIAS_UNITS[b - 2]] + 1)
                    kind = unit["table"]
                    w = TABLE_COLS[kind]
                    for h in range(4):
                        row = (unit["bias_head"] + h) * ROWS_ALL + ROW_AT[kind]
                        if unit["kind"] == "Q":
                            dst = bias[b % 2][:, 2 * h * w:2 * (h + 1) * w].rearrange("p (s c) -> p s c", s=2)
                            src = bass.AP(bias_rows.tensor, row, [[1, P], [ROW_LEN[kind], 2], [1, w]])
                        else:
                            dst = bias[b % 2][:, h * w:(h + 1) * w]
                            src = bass.AP(bias_rows.tensor, row, [[1, P], [1, w]])
                        sp.dma_start(dst, src).then_inc(bias_loaded[b % 2], 16)

            def load_item(l, it):
                item = ITEMS[it]
                unit, t, hp = item["unit"], item["t"], item["hp"]
                n = l * N_ITEMS + it
                if it >= Q_SLOTS:
                    sp.wait_ge(scored, l * N_STEPS + ITEMS[it - Q_SLOTS]["step"] + 1)
                b0, nb = (unit["q"], 4) if hp is None else (unit["q"] + 2 * hp, 2)
                sp.dma_start(q_t[:, n % Q_SLOTS, 0:nb, :].bitcast(F32).rearrange("p h c -> p (h c)"),
                             heads_t[t, :, b0 * P:(b0 + nb) * P]).then_inc(q_loaded[n % Q_SLOTS], 16)
                if it == Q_SLOTS - 1:
                    chunk_used(sp, l * CHUNKS + CHUNKS_IN - 1)
                    for first in range(Q_SLOTS - 1):
                        load_gate(l, first)
                if it >= Q_SLOTS - 1 and item["kind"] != "Q":
                    load_gate(l, it)
                if item["kind"] == "C":
                    m = l * N_MERGES + item["merge_no"]
                    if m % N_MERGES == 0:
                        for i in range(PART_SLOTS):
                            sp.wait_ge(part_stored[i], 16 * (l + 1) * (N_QUADS // PART_SLOTS))
                    if m >= MERGE_SLOTS:
                        sp.wait_ge(merge_chain, 7 * (m - MERGE_SLOTS + 1))
                    sp.dma_start(part_in[:, m % MERGE_SLOTS, :, :],
                                 part_rows[t * P:(t + 1) * P, :, unit["j"], hp, :]).then_inc(part_loaded[m % MERGE_SLOTS], 16)

            def load_gate(l, it):
                item = ITEMS[it]
                g = l * N_PAIRS + item["pair_no"]
                if item["pair_no"] >= GATE_SLOTS:
                    sp.wait_ge(mixed, g - GATE_SLOTS + 1)
                if item["kind"] == "C":
                    gates_in_dram(sp, (l + 1) * len(GATE_TILES) // DEPTH)
                col = (item["unit"]["gate"] + item["hp"]) * P
                sp.dma_start(gate[:, g % GATE_SLOTS, :], gate_rows[item["t"] * P:(item["t"] + 1) * P, col:col + P])\
                    .then_inc(gate_loaded[g % GATE_SLOTS], 16)

            def store_part(l, it):
                item = ITEMS[it]
                unit = item["unit"]
                q = l * N_QUADS + item["quad_no"]
                sp.wait_ge(part_taken, q + 1)
                first, step = token_order(item["t"], True)
                row = 2 * KV_C * 2 * PART
                dst = bass.AP(part_rows.tensor, first * row + ((unit["g"] - 1) * KV_C + unit["j"]) * 2 * PART,
                              [[step * row, P], [1, 2 * PART]])
                sp.dma_start(dst, part_out[:, q % PART_SLOTS, :, :].rearrange("p h n -> p (h n)"))\
                    .then_inc(part_stored[q % PART_SLOTS], 16)

            def load_x(l, s):
                for (lo, hi), src in zip(SEQ_TILES, x_slab(l, s, False)):
                    sp.dma_start(x_cols[:, s, lo:hi, :], src.rearrange("(t p) n -> p t n", p=P)).then_inc(x_loaded[s], 16)

            def store_x(l, s):
                sp.wait_ge(acc_added, (l * NS_OUT + s + 1) * TT)
                for (lo, hi), dst in zip(SEQ_TILES, x_slab(l, s, True)):
                    sp.dma_start(dst.rearrange("(t p) n -> p t n", p=P), x_cols[:, s, lo:hi, :]).then_inc(x_stored, 16)

            def load_tables(l):
                sp.dma_start(rope_t[:], rope).then_inc(rope_loaded, 16)
                for i, g in enumerate((q_norm_a, k_norm_a, q_norm_b, k_norm_b, q_norm_c, k_norm_c)):
                    sp.dma_start(gains[:, i, :], g[l, :].partition_broadcast(P)).then_inc(gains_loaded, 16)

            def turn_rstd(l):
                sp.wait_ge(x_chain, 4 * l + 4)
                sp.dma_start(rstd_rows.rearrange("(t p) -> p t", p=P), x_stat[:, 0, :],
                             allow_slow_non_contiguous=True).then_inc(x_rstd_stored, 16)
                sp.wait_ge(x_rstd_stored, 16 * (l + 1))
                for lo, hi in SEQ_TILES:
                    sp.dma_start(x_stat[:, 1, lo:hi], bass.AP(rstd_rows.tensor, lo * P, [[hi - lo, P], [1, hi - lo]]))\
                        .then_inc(x_rstd_back, 16)

            for l in range(DEPTH):
                if l == 0:
                    sp.dma_start(ln_rows[:], ln_g.rearrange("l (k p) -> (l k) p", p=P)).then_inc(ln_loaded, 16)
                    load_x(0, 0)
                    load_weights(0, 0)
                    load_setup()
                    load_x(0, 1)
                    load_weights(0, 1)
                    load_x(0, 2)
                    load_weights(0, 2)
                    load_x(0, 3)
                    load_tables(0)
                    sp.wait_ge(rows_copied, ROW_PIECES)
                    sp.dma_start(bias_rows, rows_sb[:]).then_inc(rows_stored, 16)
                for slot in range(CHUNKS_IN + 1):
                    if slot % PER_LOAD == 0 and slot < CHUNKS_IN:
                        load_weights(l, slot // PER_LOAD + W_RAW)
                    if slot == KC:
                        turn_rstd(l)
                    stores(l, slot)
                heads_in_dram(sp, l)
                if l == 0:
                    sp.wait_ge(rows_stored, 16)
                gates_in_dram(sp, (l + 1) * len(GATE_TILES) // DEPTH - TT)
                load_unit(l, 0)
                load_unit(l, len(OTHERS))
                for it, item in enumerate(ITEMS):
                    load_item(l, it)
                    if 2 <= it < 2 + TT:
                        store_gate(l, NS_IN - 1, it - 2)
                    for u in LOAD_AT.get(it, ()):
                        load_unit(l, u)
                    if it >= PART_DELAY and ITEMS[it - PART_DELAY]["kind"] == "Q":
                        store_part(l, it - PART_DELAY)
                sp.wait_ge(mix_lo, (l + 1) * N_PAIRS)
                sp.wait_ge(x_stored, 16 * l * X_STORES)
                for s in range(NS_OUT):
                    load_x(l, s)
                if l + 1 < DEPTH:
                    load_tables(l + 1)
                for s in range(NS_OUT):
                    for q in range(KC // PER_LOAD):
                        m = LOADS_IN + s * (KC // PER_LOAD) + q + W_RAW
                        if m < LOADS:
                            load_weights(l, m)
                        elif l + 1 < DEPTH:
                            load_weights(l + 1, m - LOADS)
                        if q == 1 and s >= 1:
                            store_x(l, s - 1)
                store_x(l, NS_OUT - 1)
            sp.wait_ge(x_stored, 16 * DEPTH * X_STORES)

        @block.tensor
        def _(pe):
            pe.wait_ge(ident_loaded, 16)

            def bias_row_pieces():
                pe.wait_ge(set_dve, 1)
                pe.wait_ge(set_loaded, SET_LOADS)
                for i in range(ROW_PIECES):
                    a, b = i * SLAB, min(ROWS_ALL, (i + 1) * SLAB)
                    pe.matmul(acc[i][0:N_BIAS, 0:b - a], rb_sb[:], sel_sb[:, a:b], start=True, stop=True)\
                        .then_inc(rows_done, 1)
                pe.wait_ge(rows_copied, ROW_PIECES)

            def turn_into(i):
                if i >= TURN_BANKS:
                    turn_evacuated(pe, i - TURN_BANKS)
                return turn_bank[i % TURN_BANKS]

            def norm_turns(l, k):
                s, j = divmod(k, KC // NS_OUT)
                for g in range(NORM_GROUPS):
                    tiles = (g + 1) * NORM_TILES
                    if l == 0:
                        pe.wait_ge(x_loaded[s], 32)
                    else:
                        pe.wait_ge(acc_added, (l * NS_OUT - NS_OUT + s) * TT + tiles)
                    i = TURN_AT[l, "norm", k, g]
                    dst = turn_into(i)
                    for t in range(NORM_TILES):
                        last = pe.transpose(dst[:, t * P:(t + 1) * P],
                                            x_cols[:, s, g * NORM_TILES + t, j * P:(j + 1) * P], ident[:])
                    last.then_inc(turn_done, 1)

            def head_turns(l, s, t):
                if not HEAD_RUNS[s]:
                    return
                n = HEAD_AT[l, s, t]
                pe.wait_ge(lo_split, n + 1)
                for b in range(0, SLAB_BLOCKS[s], 4):
                    i = TURN_AT[l, s, t, b]
                    dst = turn_into(i)
                    for j in range(b, min(b + 4, SLAB_BLOCKS[s])):
                        last = pe.transpose(dst[:, (j - b) * P:(j - b + 1) * P], pairs[:, n % 2, j, :].bitcast(F32), ident[:])
                    last.then_inc(turn_done, 1)

            def project_chunk(l, c):
                s, k = divmod(c, KC)
                n = l * CHUNKS + c
                pe.wait_ge(w_lo_done, n + 1)
                if s == 0:
                    pe.wait_ge(norm_lo, (l * KC + k + 1) * NORM_GROUPS)
                for t in range(TT):
                    if k == 0:
                        if 0 < s <= NS_IN:
                            pe.wait_ge(acc_copied, (l * NS_IN + s - 1) * TT + t + 1)
                        elif s > NS_IN:
                            pe.wait_ge(acc_added, (l * NS_OUT + s - NS_IN - 1) * TT + t + 1)
                        elif l > 0:
                            pe.wait_ge(acc_added, (l * NS_OUT - 1) * TT + t + 1)
                    hi, lo = (tokens_of(a, k, t, s in INTERLEAVED) for a in (act_hi, act_lo))
                    pe.matmul(acc[t][:], hi, w_hi[:, n % W_RING, :], start=(k == 0), stop=False)
                    pe.matmul(acc[t][:], hi, w_lo[:, n % W_RING, :], start=False, stop=False)
                    last = pe.matmul(acc[t][:], lo, w_hi[:, n % W_RING, :], start=False, stop=(k == KC - 1))
                    if k == KC - 1:
                        last.then_inc(acc_done, 1)
                if k < KC - 1:
                    last.then_inc(w_used, 1)

            def scores(l, i):
                st = STEPS[i]
                n = l * N_STEPS + i
                it = l * N_ITEMS + st["item"]
                if st["r"] != 1:
                    pe.wait_ge(q_loaded[it % Q_SLOTS], 16 * (it // Q_SLOTS + 1))
                    if st["t"] == 0 and st["hp"] != 1:
                        slot, times = kv_place(l, st["u"])
                        pe.wait_ge(kv_loaded[slot], 16 * 5 * times)
                if i >= S_BANKS:
                    pe.wait_ge(exped if STEPS[i - S_BANKS]["kind"] == "B" else biased, n - S_BANKS + 1)
                keys = k_t[:, kv_place(l, st["u"])[0], :, :, :]
                dst = s_bank[n % S_BANKS]
                if st["kind"] == "Q":
                    for h in range(4):
                        q, out = q_t[:, it % Q_SLOTS, h, :], dst[:, h * P:(h + 1) * P]
                        pe.matmul(out, q, keys[:, st["a"], 0, :], start=True, stop=False)
                        last = pe.matmul(out, q, keys[:, st["a"], 1, :], start=False, stop=True)
                else:
                    q, out = q_t[:, it % Q_SLOTS, st["r"], :], dst[:, 0:st["tiles"] * P]
                    pe.matmul(out, q, keys[:, st["a"]:st["b"], 0, :], start=True, stop=False)
                    last = pe.matmul(out, q, keys[:, st["a"]:st["b"], 1, :], start=False, stop=True)
                last.then_inc(scored, 1)

            def p_turn(l, i):
                st = STEPS[i]
                n = l * N_STEPS + i
                pe.wait_ge(exped, n + 1)
                if i >= PT_BANKS:
                    prob_copied(pe, l, i - PT_BANKS)
                for j in range(st["tiles"]):
                    last = pe.transpose(pt_bank[n % PT_BANKS][:, j * P:(j + 1) * P],
                                        prob[:, n % P_SLOTS, j * P:(j + 1) * P], ident[:])
                last.then_inc(p_turned, 1)

            def pv(l, i):
                st = STEPS[i]
                n = l * N_STEPS + i
                it = st["item"]
                prob_copied(pe, l, i)
                if st["r"] != 1 and it >= 2:
                    old = ITEMS[it - 2]
                    if old["kind"] == "Q":
                        pe.wait_ge(part_taken, l * N_QUADS + old["quad_no"] + 1)
                    else:
                        pe.wait_ge(mixed, l * N_PAIRS + old["pair_no"] + 1)
                values = v_t[:, kv_place(l, st["u"])[0], :, :]
                for j in range(st["tiles"]):
                    if st["kind"] == "Q":
                        head, kt, first, end = j, st["a"], True, True
                    else:
                        head, kt, first, end = st["r"], st["a"] + j, j == 0, j == st["tiles"] - 1
                    last = pe.matmul(o_bank[it % 2][:, head * DH:(head + 1) * DH], prob_t[:, n % PT_SLOTS, j * P:(j + 1) * P],
                                     values[:, kt, :], start=first, stop=end)
                last.then_inc(pv_done, 1)

            def mix_turn(l, it):
                n = l * N_PAIRS + ITEMS[it]["pair_no"]
                pe.wait_ge(mixed, n + 1)
                if n >= 1:
                    pe.wait_ge(mix_lo, n)
                pe.transpose(mix_bank[:, 0:P], mix[:, n % 2, :], ident[:]).then_inc(mix_turned, 1)

            for l in range(DEPTH):
                if l == 0:
                    pe.wait_ge(ln_loaded, 16)
                    pe.transpose(acc[5][:, 0:DEPTH * KC], ln_rows[:], ident[0:DEPTH * KC, 0:DEPTH * KC]).then_inc(ln_turned, 1)
                    for k in range(NORM_LEAD):
                        norm_turns(0, k)
                    bias_row_pieces()
                for slot in range(CHUNKS_IN):
                    if l == 0 and slot + NORM_LEAD < KC:
                        norm_turns(0, slot + NORM_LEAD)
                    project_chunk(l, slot)
                    if l > 0 and slot < KC - NORM_EARLY:
                        norm_turns(l, NORM_EARLY + slot)
                    for step, s, t in POST.get(slot, ()):
                        if step == "turn":
                            head_turns(l, s, t)
                pe.wait_ge(acc_copied, (l + 1) * NS_IN * TT)
                turn_evacuated(pe, LAYER_TURNS[l] - 1)
                turn_evacuated(pe, LAYER_TURNS[l] - 2)
                for i in range(N_STEPS + X_LAG):
                    if i < N_STEPS:
                        scores(l, i)
                    if 0 <= i - T_LAG < N_STEPS:
                        p_turn(l, i - T_LAG)
                    if 0 <= i - V_LAG < N_STEPS:
                        pv(l, i - V_LAG)
                    if ends_pair(i - X_LAG):
                        mix_turn(l, STEPS[i - X_LAG]["item"])
                pe.wait_ge(mix_lo, (l + 1) * N_PAIRS)
                for c in range(CHUNKS_IN, CHUNKS):
                    project_chunk(l, c)
                    k = c - (CHUNKS - KC) - 1
                    if l + 1 < DEPTH and 0 <= k < NORM_EARLY:
                        norm_turns(l + 1, k)

        @block.scalar
        def _(act):
            def split_hi(l, c):
                n = l * CHUNKS + c
                load, j = divmod(n, PER_LOAD)
                if j == 0:
                    act.wait_ge(w_loaded[load % W_RAW], LOAD_COUNT[load])
                if n >= W_RING:
                    chunk_used(act, n - W_RING)
                nc.scalar.copy(w_hi[:, n % W_RING, :], w_raw[:, load % W_RAW, j, :]).then_inc(w_hi_done, 1)

            def norm_squares(l, s):
                if l == 0:
                    act.wait_ge(x_loaded[s], 32)
                else:
                    act.wait_ge(acc_added, ((l - 1) * NS_OUT + s + 1) * TT)
                    if s == 0:
                        act.wait_ge(x_chain, 4 * l)
                for t in range(TT):
                    n = (l * NS_OUT + s) * TT + t
                    if n >= 2:
                        act.wait_ge(x_squared, n - 1)
                    nc.scalar.activation(junk[:, n % 2, :], x_cols[:, s, t, :], ACT.Square,
                                         accum_out=x_sums[:, t, s:s + 1]).then_inc(x_squared, 1)

            def norm_hi_parts(l, k):
                for g in range(NORM_GROUPS):
                    i = TURN_AT[l, "norm", k, g]
                    act.wait_ge(turn_done, i + 1)
                    if i == 0:
                        act.wait_ge(ln_copied, 1)
                    cols = slice(g * NORM_TILES * P, (g + 1) * NORM_TILES * P)
                    nc.scalar.activation(act_hi[:, k, cols], turn_bank[i % TURN_BANKS][:, 0:NORM_TILES * P], ACT.Copy,
                                         scale=ln_cols[:, l * KC + k:l * KC + k + 1]).then_inc(norm_hi, 1)

            def drain(l, s, t):
                n = (l * NS_IN + s) * TT + t
                act.wait_ge(acc_done, (l * (NS_IN + NS_OUT) + s) * TT + t + 1)
                if s == 0 and t == 0:
                    act.wait_ge(x_chain, 4 * l + 4)
                    act.wait_ge(x_stored, 16 * l * X_STORES)
                if s == INTERLEAVED[0] and t == 0:
                    act.wait_ge(x_rstd_back, 16 * len(SEQ_TILES) * (l + 1))
                if s > 0:
                    if HEAD_RUNS[s - 1]:
                        act.wait_ge(scaled, HEAD_AT[l, s - 1, t] + 1)
                    if GATE_RUNS[s - 1]:
                        act.wait_ge(gates_stored, 16 * (GATE_AT[l, s - 1, TT - 1] + 1))
                    if V_RUNS[s - 1]:
                        act.wait_ge(v_stored, 16 * v_stores_through(l, s - 1, TT - 1))
                order = 1 if s in INTERLEAVED else 0
                for func, a, b in drain_parts(s):
                    ins = nc.scalar.activation(raw[:, t, a:b], acc[t][:, a:b], func, scale=x_stat[:, order, t:t + 1])
                ins.then_inc(acc_copied, 1)

            def squares(l, s, t):
                n = HEAD_AT[l, s, t]
                a, b = head_cols(s)
                act.wait_ge(acc_copied, (l * NS_IN + s) * TT + t + 1)
                if n >= 2:
                    act.wait_ge(summed, n - 1)
                nc.scalar.activation(sq[:, n % 2, a:b], raw[:, t, a:b], ACT.Square).then_inc(squared, 1)

            def head_hi(l, s, t):
                n = HEAD_AT[l, s, t]
                rotated_ready(act, l, s, t)
                if n >= 2:
                    ll, ss, tt = HEAD_TILES[n - 2]
                    act.wait_ge(turn_done, TURN_AT[ll, ss, tt, (SLAB_BLOCKS[ss] - 1) // 4 * 4] + 1)
                src, hi, _ = block_views(s, n)
                nc.scalar.copy(hi, src).then_inc(hi_split, 1)

            def head_copy(l, s, t):
                n = HEAD_AT[l, s, t]
                for b in range(0, SLAB_BLOCKS[s], 4):
                    i = TURN_AT[l, s, t, b]
                    if turn_on_act(i):
                        copy_turned(act, nc.scalar.copy, i, n, s, b).then_inc(turn_act, 1)

            def exp_step(l, i):
                st = STEPS[i]
                n = l * N_STEPS + i
                act.wait_ge(biased, n + 1)
                if st["kind"] == "Q":
                    q = (l * N_QUADS + ITEMS[st["item"]]["quad_no"]) % PART_SLOTS
                    for h in range(4):
                        v = prob[:, n % P_SLOTS, h * P:(h + 1) * P]
                        at = 2 * DH + h % 2
                        ins = nc.scalar.activation(v, v, ACT.Exp, bias=part_out[:, q, h // 2, at:at + 1], scale=-1.0,
                                                   accum_out=part_out[:, q, h // 2, at + 2:at + 3])
                    ins.then_inc(exped, 1)
                    return
                pair = l * N_PAIRS + ITEMS[st["item"]]["pair_no"]
                cols = st["tiles"] * P + (1 if st["kind"] == "A" else 0)
                dst = src = prob[:, n % P_SLOTS, 0:cols]
                if st["kind"] == "A":
                    act.wait_ge(sunk, l * SUNK[-1] + SUNK[i])
                if st["kind"] == "B":
                    src = s_bank[n % S_BANKS][:, 0:cols]
                if pair >= STAT_SLOTS:
                    act.wait_ge(mixed, pair - STAT_SLOTS + 1)
                s, r = pair % STAT_SLOTS, st["r"]
                nc.scalar.activation(dst, src, ACT.Exp, bias=minus_max[:, s, r:r + 1], scale=-1.0,
                                     accum_out=denom[:, s, r:r + 1]).then_inc(exped, 1)

            def pt_copy(l, i):
                if on_act(i):
                    copy_pt(act, nc.scalar.copy, l, i).then_inc(pt_act, 1)

            def merge_exp(l, it):
                m = l * N_MERGES + ITEMS[it]["merge_no"]
                act.wait_ge(merge_args, 2 * m + 2)
                v = merge_w[:, m % MERGE_SLOTS, :, :].rearrange("p g h -> p (g h)")
                nc.scalar.activation(v, v, ACT.Exp).then_inc(merge_exps, 1)

            def mix_hi_part(l, it):
                item = ITEMS[it]
                chunk, t = item["unit"]["gate"] + item["hp"], item["t"]
                act.wait_ge(mix_turned, l * N_PAIRS + item["pair_no"] + 1)
                nc.scalar.copy(act_hi[:, chunk, t * P:(t + 1) * P], mix_bank[:, 0:P]).then_inc(mix_hi, 1)

            for l in range(DEPTH):
                if l == 0:
                    for k in range(NORM_LEAD):
                        norm_hi_parts(0, k)
                    for c in range(LEAD):
                        split_hi(0, c)
                for slot in range(CHUNKS_IN + 1):
                    if l == 0 and slot + NORM_LEAD < KC:
                        norm_hi_parts(0, slot + NORM_LEAD)
                    if slot + LEAD < CHUNKS_IN:
                        split_hi(l, slot + LEAD)
                    if l == 0 and slot in SQUARE_SLOTS:
                        norm_squares(0, SQUARE_SLOTS.index(slot))
                    if l > 0 and 0 <= slot - 1 < KC - NORM_EARLY:
                        norm_hi_parts(l, NORM_EARLY + slot - 1)
                    if l > 0 and slot == KC - NORM_EARLY + 1:
                        norm_squares(l, NS_OUT - 1)
                    for step, s, t in POST.get(slot, ()):
                        if step == "drain":
                            drain(l, s, t)
                    for step, s, t in POST.get(slot, ()):
                        if step == "sums" and HEAD_RUNS[s]:
                            squares(l, s, t)
                        if step == "split" and HEAD_RUNS[s]:
                            head_hi(l, s, t)
                        if step == "store" and HEAD_RUNS[s]:
                            head_copy(l, s, t)
                chunk_used(act, l * CHUNKS + CHUNKS_IN - 1)
                heads_in_dram(act, l)
                for i in range(N_STEPS + LO_LAG):
                    if 0 <= i - T_LAG < N_STEPS:
                        pt_copy(l, i - T_LAG)
                    if i < N_STEPS:
                        exp_step(l, i)
                    if ends_merge(i - MERGE_LAG):
                        merge_exp(l, STEPS[i - MERGE_LAG]["item"])
                    if ends_pair(i - X_LAG):
                        mix_hi_part(l, STEPS[i - X_LAG]["item"])
                act.wait_ge(mix_lo, (l + 1) * N_PAIRS)
                for c in range(LEAD):
                    split_hi(l, CHUNKS_IN + c)
                for c in range(CHUNKS_OUT):
                    s, k = divmod(c, KC)
                    if l + 1 < DEPTH or c + LEAD < CHUNKS_OUT:
                        split_hi(l, CHUNKS_IN + c + LEAD)
                    if l + 1 < DEPTH:
                        if s > 0 and k == KC // 2:
                            norm_squares(l + 1, s - 1)
                        if s == NS_OUT - 1 and 0 <= k - 2 < NORM_EARLY:
                            norm_hi_parts(l + 1, k - 2)

        @block.vector
        def _(dve):
            nc.vector.memset(rb_sb[BUCKETS:BUCKETS + 1, :], 1.0).then_inc(set_dve, 1)
            dve.wait_ge(ln_turned, 1)
            nc.vector.tensor_copy(ln_cols[:], acc[5][:, 0:DEPTH * KC]).then_inc(ln_copied, 1)
            dve.wait_ge(ln_copied, 1)

            def copy_bias_rows():
                for i in range(ROW_PIECES):
                    a, b = i * SLAB, min(ROWS_ALL, (i + 1) * SLAB)
                    dve.wait_ge(rows_done, i + 1)
                    nc.vector.tensor_copy(rows_sb[:, a:b], acc[i][0:N_BIAS, 0:b - a]).then_inc(rows_copied, 1)
                nc.vector.tensor_scalar(sinks[:], sinks[:], -1.0, None, ALU.mult).then_inc(set_dve, 1)
                dve.wait_ge(set_dve, 2)

            def scale_gains(l):
                dve.wait_ge(gains_loaded, 16 * 6 * (l + 1))
                v = gains[:, 0:6:2, :]
                nc.vector.tensor_scalar(v, v, -float(DH) ** -0.5, None, ALU.mult).then_inc(gains_scaled, 1)

            def split_lo(l, c):
                n = l * CHUNKS + c
                load, j = divmod(n, PER_LOAD)
                dve.wait_ge(w_hi_done, n + 1)
                nc.vector.tensor_tensor(w_lo[:, n % W_RING, :], w_raw[:, load % W_RAW, j, :],
                                        w_hi[:, n % W_RING, :].bitcast(F32), ALU.subtract).then_inc(w_lo_done, 1)

            def norm_lo_parts(l, k):
                if l == 0 and k == KC // 2:
                    dve.wait_ge(rows_stored, 16)
                for g in range(NORM_GROUPS):
                    i = TURN_AT[l, "norm", k, g]
                    dve.wait_ge(norm_hi, NORM_AT[l, "norm", k, g] + 1)
                    cols = slice(g * NORM_TILES * P, (g + 1) * NORM_TILES * P)
                    nc.vector.scalar_tensor_tensor(
                        out=act_lo[:, k, cols], in0=turn_bank[i % TURN_BANKS][:, 0:NORM_TILES * P],
                        scalar=ln_cols[:, l * KC + k:l * KC + k + 1], in1=act_hi[:, k, cols].bitcast(F32),
                        op0=ALU.mult, op1=ALU.subtract).then_inc(norm_lo, 1)

            def sums(l, s, t):
                n = HEAD_AT[l, s, t]
                a, b = head_cols(s)
                dve.wait_ge(squared, n + 1)
                if n >= TT:
                    dve.wait_ge(scaled, n - TT + 1)
                nc.vector.tensor_reduce(stats[:, t, 0:(b - a) // DH], sq[:, n % 2, a:b].rearrange("p (h d) -> p h d", d=DH),
                                        AX_X, ALU.add).then_inc(summed, 1)

            def scale(l, s, t):
                n = HEAD_AT[l, s, t]
                a, b = head_cols(s)
                dve.wait_ge(rstd_done, n + 1)
                if n >= 2:
                    dve.wait_ge(lo_split, n - 1)
                m = (b - a) // DH
                nc.vector.tensor_tensor(y[:, n % 2, a:b].rearrange("p (h d) -> p h d", d=DH),
                                        raw[:, t, a:b].rearrange("p (h d) -> p h d", d=DH),
                                        stats[:, t, 0:m].unsqueeze(2).broadcast_to([P, m, DH]), ALU.mult)\
                    .then_inc(scaled, 1)

            def rotate(l, s, t):
                n, k = HEAD_AT[l, s, t], ROPE_AT[l, s, t]
                a, b = head_cols(s)
                m = (b - a) // DH
                pos = t if t < 2 else t - 2
                dve.wait_ge(gained, n + 1)
                dve.wait_ge(rope_loaded, 16 * (l + 1))
                cos = rope_t[:, pos, 0, :].unsqueeze(1).broadcast_to([P, m, DH])
                yv = y[:, n % 2, a:b]
                rv, sv = rot[:, 0, a:b], rot[:, 1, a:b]
                q = N_FREQ
                y5 = yv.rearrange("p (h x c f) -> p h x c f", x=2, c=2, f=q)
                s5 = sv.rearrange("p (h x c f) -> p h x c f", x=2, c=2, f=q)
                sin4 = rope_t[:, pos, 1, :].rearrange("p (x c f) -> p x c f", x=2, c=2)
                if k > 0:
                    dve.wait_ge(roped, 5 * k)
                nc.vector.tensor_tensor(rv.rearrange("p (h d) -> p h d", d=DH), yv.rearrange("p (h d) -> p h d", d=DH),
                                        cos, ALU.mult).then_inc(roped, 1)
                for c in range(2):
                    sin = sin4[:, :, c, :].unsqueeze(1).broadcast_to([P, m, 2, q])
                    nc.vector.tensor_tensor(s5[:, :, :, c, :], y5[:, :, :, 1 - c, :], sin, ALU.mult).then_inc(roped, 1)
                dve.wait_ge(roped, 5 * k + 3)
                nc.vector.tensor_tensor(yv, rv, sv, ALU.add).then_inc(roped, 2)

            def head_lo(l, s, t):
                n = HEAD_AT[l, s, t]
                dve.wait_ge(hi_split, n + 1)
                src, hi, lo = block_views(s, n)
                nc.vector.tensor_tensor(lo, src, hi.bitcast(F32), ALU.subtract).then_inc(lo_split, 1)

            def head_copy(l, s, t):
                n = HEAD_AT[l, s, t]
                for b in range(0, SLAB_BLOCKS[s], 4):
                    i = TURN_AT[l, s, t, b]
                    if not turn_on_act(i):
                        copy_turned(dve, nc.vector.tensor_copy, i, n, s, b).then_inc(turn_dve, 1)

            def find_minima(l, i):
                st = STEPS[i]
                n = l * N_STEPS + i
                unit, kind, width = st["unit"], st["kind"], st["tiles"] * P
                dve.wait_ge(scored, n + 1)
                if i >= P_SLOTS:
                    dve.wait_ge(p_turned, n - P_SLOTS + 1)
                src = s_bank[n % S_BANKS]
                if kind != "B":
                    b = BIAS_NO[st["u"]]
                    table = bias[b % 2]
                    if st["t"] == 0 and st["hp"] != 1 and st["r"] != 1:
                        bias_in(dve, l, b)
                if kind == "Q":
                    q = l * N_QUADS + ITEMS[st["item"]]["quad_no"]
                    if q == l * N_QUADS:
                        gates_in_dram(dve, (l + 1) * len(GATE_TILES) // DEPTH)
                    if q >= PART_SLOTS:
                        dve.wait_ge(part_stored[q % PART_SLOTS], 16 * (q // PART_SLOTS))
                    for h in range(4):
                        last_col = (2 * h + (1 if st["t"] >= SEQ_TILES[1][0] else 0)) * P + P - 1
                        ins = nc.vector.tensor_tensor_reduce(
                            prob[:, n % P_SLOTS, h * P:(h + 1) * P], src[:, h * P:(h + 1) * P],
                            bass.AP(table, last_col, [[BIAS_COLS, P], [-1, P]]), 1.0, 3e38, ALU.add, ALU.min,
                            part_out[:, q % PART_SLOTS, h // 2, 2 * DH + h % 2:2 * DH + h % 2 + 1])
                    ins.then_inc(biased, 1)
                    return
                pair = l * N_PAIRS + ITEMS[st["item"]]["pair_no"]
                if pair >= STAT_SLOTS:
                    dve.wait_ge(mixed, pair - STAT_SLOTS + 1)
                least = minus_max[:, pair % STAT_SLOTS, st["r"]:st["r"] + 1]
                if kind == "B":
                    nc.vector.tensor_reduce(least, src[:, 0:width], AX_X, ALU.min).then_inc(biased, 1)
                    return
                first = 3e38
                if kind == "A":
                    head = l * H_A + unit["bias_head"] + 2 * st["hp"] + st["r"]
                    first = sinks[:, head:head + 1]
                    nc.vector.tensor_copy(prob[:, n % P_SLOTS, width:width + 1], first).then_inc(sunk, 1)
                cols = TABLE_COLS[unit["table"]]
                last_col = (2 * st["hp"] + st["r"] + 1) * cols - 1 - (st["a"] - (st["t"] - 1)) * P
                nc.vector.tensor_tensor_reduce(prob[:, n % P_SLOTS, 0:width], src[:, 0:width],
                                               bass.AP(table, last_col, [[BIAS_COLS, P], [-1, width]]),
                                               1.0, first, ALU.add, ALU.min, least).then_inc(biased, 1)

            def pt_copy(l, i):
                if not on_act(i):
                    copy_pt(dve, nc.vector.tensor_copy, l, i).then_inc(pt_dve, 1)

            def take_part(l, it):
                q = l * N_QUADS + ITEMS[it]["quad_no"]
                dve.wait_ge(pv_done, l * N_STEPS + ITEMS[it]["step"] + 1)
                nc.vector.tensor_copy(part_out[:, q % PART_SLOTS, :, 0:2 * DH],
                                      o_bank[it % 2][:, 0:4 * DH].rearrange("p (h n) -> p h n", h=2)).then_inc(part_taken, 1)

            def merge_minima(l, it):
                item = ITEMS[it]
                m, pair = l * N_MERGES + item["merge_no"], l * N_PAIRS + item["pair_no"]
                slot = m % MERGE_SLOTS
                dve.wait_ge(part_loaded[slot], 16 * (m // MERGE_SLOTS + 1))
                if m >= MERGE_SLOTS:
                    dve.wait_ge(merge_args, 2 * (m - MERGE_SLOTS + 1))
                least = merge_min[:, slot, :]
                nc.vector.tensor_tensor(least, part_in[:, slot, 0, 2 * DH:2 * DH + 2], part_in[:, slot, 1, 2 * DH:2 * DH + 2],
                                        ALU.min).then_inc(merge_mins, 1)
                dve.wait_ge(merge_mins, 2 * m + 1)
                dve.wait_ge(biased, l * N_STEPS + item["step"] + 1)
                nc.vector.tensor_tensor(least, least, minus_max[:, pair % STAT_SLOTS, :], ALU.min).then_inc(merge_mins, 1)

            def finish_item(l, it):
                item = ITEMS[it]
                n = l * N_PAIRS + item["pair_no"]
                o = o_bank[it % 2]
                if item["kind"] != "C":
                    dve.wait_ge(exped, l * N_STEPS + item["step"] + 1)
                    nc.vector.reciprocal(recip[:, n % 2, :], denom[:, n % STAT_SLOTS, :]).then_inc(recips, 1)
                    dve.wait_ge(recips, n + 1)
                dve.wait_ge(pv_done, l * N_STEPS + item["step"] + 1)
                dve.wait_ge(gate_loaded[n % GATE_SLOTS], 16 * (n // GATE_SLOTS + 1))
                if n >= 2:
                    dve.wait_ge(mix_turned, n - 1)
                if item["kind"] == "C":
                    m = l * N_MERGES + item["merge_no"]
                    dve.wait_ge(merge_chain, 7 * m + 7)
                    for r in range(2):
                        cols = slice(r * DH, (r + 1) * DH)
                        ins = nc.vector.scalar_tensor_tensor(
                            out=mix[:, n % 2, cols], in0=o[:, cols], scalar=merge_w[:, m % MERGE_SLOTS, 2, r:r + 1],
                            in1=part_sum[:, m % 2, 0, cols], op0=ALU.mult, op1=ALU.add)
                    ins.then_inc(recips, 1)
                    dve.wait_ge(recips, n + 1)
                    nc.vector.tensor_tensor(mix[:, n % 2, :], mix[:, n % 2, :], gate[:, n % GATE_SLOTS, :], ALU.mult)\
                        .then_inc(mixed, 1)
                    return
                for r in range(2):
                    cols = slice(r * DH, (r + 1) * DH)
                    ins = nc.vector.scalar_tensor_tensor(
                        out=mix[:, n % 2, cols], in0=o[:, cols], scalar=recip[:, n % 2, r:r + 1],
                        in1=gate[:, n % GATE_SLOTS, cols], op0=ALU.mult, op1=ALU.mult)
                ins.then_inc(mixed, 1)

            def mix_lo_part(l, it):
                item = ITEMS[it]
                chunk = item["unit"]["gate"] + item["hp"]
                dve.wait_ge(mix_hi, l * N_PAIRS + item["pair_no"] + 1)
                cols = slice(item["t"] * P, (item["t"] + 1) * P)
                nc.vector.tensor_tensor(act_lo[:, chunk, cols], mix_bank[:, 0:P], act_hi[:, chunk, cols].bitcast(F32),
                                        ALU.subtract).then_inc(mix_lo, 1)

            def add_residual(l, s, t):
                dve.wait_ge(acc_done, (l * (NS_IN + NS_OUT) + NS_IN + s) * TT + t + 1)
                if t == 0:
                    dve.wait_ge(x_loaded[s], 32 * (l + 2))
                v = x_cols[:, s, t, :]
                nc.vector.tensor_tensor(v, acc[t][:], v, ALU.add).then_inc(acc_added, 1)

            for l in range(DEPTH):
                if l == 0:
                    for k in range(NORM_LEAD):
                        norm_lo_parts(0, k)
                    copy_bias_rows()
                    for c in range(LEAD):
                        split_lo(0, c)
                else:
                    for t in range(TT):
                        add_residual(l - 1, NS_OUT - 1, t)
                for slot in range(CHUNKS_IN + 1):
                    if l == 0 and slot + NORM_LEAD < KC:
                        norm_lo_parts(0, slot + NORM_LEAD)
                    if slot + LEAD < CHUNKS_IN:
                        split_lo(l, slot + LEAD)
                    if l > 0 and 0 <= slot - 1 < KC - NORM_EARLY:
                        norm_lo_parts(l, NORM_EARLY + slot - 1)
                    if slot == KC - 2:
                        scale_gains(l)
                    for step, s, t in POST.get(slot, ()):
                        if step == "sums" and HEAD_RUNS[s]:
                            sums(l, s, t)
                        if step == "scale" and HEAD_RUNS[s]:
                            scale(l, s, t)
                        if step == "rope" and (l, s, t) in ROPE_AT:
                            rotate(l, s, t)
                        if step == "split" and HEAD_RUNS[s]:
                            head_lo(l, s, t)
                        if step == "store" and HEAD_RUNS[s]:
                            head_copy(l, s, t)
                chunk_used(dve, l * CHUNKS + CHUNKS_IN - 1)
                heads_in_dram(dve, l)
                for i in range(N_STEPS + LO_LAG):
                    if i < N_STEPS:
                        find_minima(l, i)
                    if 0 <= i - T_LAG < N_STEPS:
                        pt_copy(l, i - T_LAG)
                    if ends_merge(i - MIN_LAG):
                        merge_minima(l, STEPS[i - MIN_LAG]["item"])
                    if ends_pair(i - MIX_LAG):
                        finish_item(l, STEPS[i - MIX_LAG]["item"])
                    if ends_quad(i - MIX_LAG):
                        take_part(l, STEPS[i - MIX_LAG]["item"])
                    if ends_pair(i - LO_LAG):
                        mix_lo_part(l, STEPS[i - LO_LAG]["item"])
                for c in range(LEAD):
                    split_lo(l, CHUNKS_IN + c)
                for c in range(CHUNKS_OUT):
                    s, k = divmod(c, KC)
                    if s > 0 and k == 0:
                        for t in range(TT):
                            add_residual(l, s - 1, t)
                    if l + 1 < DEPTH or c + LEAD < CHUNKS_OUT:
                        split_lo(l, CHUNKS_IN + c + LEAD)
                    if l + 1 < DEPTH and s == NS_OUT - 1 and 0 <= k - 2 < NORM_EARLY:
                        norm_lo_parts(l + 1, k - 2)
            for t in range(TT):
                add_residual(DEPTH - 1, NS_OUT - 1, t)

        @block.gpsimd
        def _(pool):
            nc.gpsimd.memset(half[:], -0.5)
            nc.gpsimd.memset(minus_one[:], -1.0).then_inc(rstd_chain, 1)
            pool.wait_ge(rstd_chain, 1)

            def norm_rstd(l):
                pool.wait_ge(x_squared, (l + 1) * NS_OUT * TT)
                if l > 0:
                    pool.wait_ge(acc_copied, l * NS_IN * TT)
                    pool.wait_ge(x_rstd_stored, 16 * l)
                v = x_stat[:, 0, :]
                nc.gpsimd.tensor_tensor(x_sums[:, :, 0:2], x_sums[:, :, 0:2], x_sums[:, :, 2:4], ALU.add).then_inc(x_chain, 1)
                pool.wait_ge(x_chain, 4 * l + 1)
                nc.gpsimd.tensor_tensor(v, x_sums[:, :, 0], x_sums[:, :, 1], ALU.add).then_inc(x_chain, 1)
                pool.wait_ge(x_chain, 4 * l + 2)
                nc.gpsimd.tensor_scalar(v, v, 1.0 / D, EPS, ALU.mult, ALU.add).then_inc(x_chain, 1)
                pool.wait_ge(x_chain, 4 * l + 3)
                nc.gpsimd.tensor_tensor(v, v, half[:, 0:TT], ALU.pow).then_inc(x_chain, 1)

            def head_rstd(l, s, t):
                n = HEAD_AT[l, s, t]
                a, b = head_cols(s)
                v = stats[:, t, 0:(b - a) // DH]
                pool.wait_ge(summed, n + 1)
                nc.gpsimd.tensor_scalar(v, v, 1.0 / DH, EPS, ALU.mult, ALU.add).then_inc(rstd_chain, 1)
                pool.wait_ge(rstd_chain, n + 2)
                nc.gpsimd.tensor_tensor(v, v, half[:, 0:(b - a) // DH], ALU.pow).then_inc(rstd_done, 1)

            def gain(l, s, t):
                n = HEAD_AT[l, s, t]
                pool.wait_ge(scaled, n + 1)
                for kind, mixer, u, m in HEAD_RUNS[s]:
                    v = y[:, n % 2, u * DH:(u + m) * DH].rearrange("p (h d) -> p h d", d=DH)
                    g = gains[:, GAIN[kind, mixer], :].unsqueeze(1).broadcast_to([P, m, DH])
                    ins = nc.gpsimd.tensor_tensor(v, v, g, ALU.mult)
                ins.then_inc(gained, 1)

            def merge(l, it):
                item = ITEMS[it]
                m, pair = l * N_MERGES + item["merge_no"], l * N_PAIRS + item["pair_no"]
                slot = m % MERGE_SLOTS
                part, w, d = part_in[:, slot, :, :], merge_w[:, slot, :, :], merge_d[:, slot, :, :]
                pool.wait_ge(merge_mins, 2 * m + 2)
                if m >= MERGE_SLOTS:
                    pool.wait_ge(mixed, pair - MERGE_SLOTS + 1)
                least = merge_min[:, slot, :]
                nc.gpsimd.tensor_tensor(w[:, 0:2, :], least.unsqueeze(1).broadcast_to([P, 2, 2]),
                                        part[:, :, 2 * DH:2 * DH + 2], ALU.subtract).then_inc(merge_args, 1)
                nc.gpsimd.tensor_tensor(w[:, 2, :], least, minus_max[:, pair % STAT_SLOTS, :], ALU.subtract)\
                    .then_inc(merge_args, 1)
                pool.wait_ge(merge_exps, m + 1)
                pool.wait_ge(exped, l * N_STEPS + item["step"] + 1)
                nc.gpsimd.tensor_tensor(d[:, 0:2, :], w[:, 0:2, :], part[:, :, 2 * DH + 2:PART], ALU.mult)
                nc.gpsimd.tensor_tensor(d[:, 2, :], w[:, 2, :], denom[:, pair % STAT_SLOTS, :], ALU.mult)\
                    .then_inc(merge_chain, 1)
                pool.wait_ge(merge_chain, 7 * m + 1)
                nc.gpsimd.tensor_tensor(d[:, 0, :], d[:, 0, :], d[:, 1, :], ALU.add).then_inc(merge_chain, 1)
                pool.wait_ge(merge_chain, 7 * m + 2)
                nc.gpsimd.tensor_tensor(d[:, 0, :], d[:, 0, :], d[:, 2, :], ALU.add).then_inc(merge_chain, 1)
                pool.wait_ge(merge_chain, 7 * m + 3)
                nc.gpsimd.tensor_tensor(d[:, 0, :], d[:, 0, :], minus_one[:, 0:2], ALU.pow).then_inc(merge_chain, 1)
                pool.wait_ge(merge_chain, 7 * m + 4)
                nc.gpsimd.tensor_tensor(w, w, d[:, 0, :].unsqueeze(1).broadcast_to([P, 3, 2]), ALU.mult)\
                    .then_inc(merge_chain, 1)
                pool.wait_ge(merge_chain, 7 * m + 5)
                if m >= 2:
                    pool.wait_ge(mixed, pair - 1)
                for r in range(2):
                    cols = slice(r * DH, (r + 1) * DH)
                    ins = nc.gpsimd.tensor_tensor(part_sum[:, m % 2, :, cols], part[:, :, cols],
                                                  w[:, 0:2, r:r + 1].broadcast_to([P, 2, DH]), ALU.mult)
                ins.then_inc(merge_chain, 1)
                pool.wait_ge(merge_chain, 7 * m + 6)
                nc.gpsimd.tensor_tensor(part_sum[:, m % 2, 0, :], part_sum[:, m % 2, 0, :], part_sum[:, m % 2, 1, :],
                                        ALU.add).then_inc(merge_chain, 1)

            for l in range(DEPTH):
                norm_rstd(l)
                pool.wait_ge(gains_scaled, l + 1)
                for slot in range(CHUNKS_IN):
                    for step, s, t in POST.get(slot, ()):
                        if step == "sums" and HEAD_RUNS[s]:
                            head_rstd(l, s, t)
                        if step == "scale" and HEAD_RUNS[s]:
                            gain(l, s, t)
                for it, item in enumerate(ITEMS):
                    if item["kind"] == "C":
                        merge(l, it)


ROW_PIECES = -(-ROWS_ALL // SLAB)
SET_LOADS = 16 * 3
V_STORES = TT * sum(len(V_RUNS[s]) for s in range(NS_IN))
X_STORES = 2 * NS_OUT
LAYER_TURNS = [sum(1 for x in TURNS if x[0] <= l) for l in range(DEPTH)]
PART_DELAY = 8


def load_counts():
    counts, now = [], [0] * W_RAW
    for n in range(DEPTH * CHUNKS // PER_LOAD):
        s = n % (CHUNKS // PER_LOAD) // (KC // PER_LOAD)
        now[n % W_RAW] += 16 * (len(pieces_of(s)) if s < NS_IN else 1)
        counts.append(now[n % W_RAW])
    return counts


LOAD_COUNT = load_counts()


_INS = ["x_prompt", "x_sample", "ln_g", "w_in", "q_norm_a", "k_norm_a", "sink_a", "q_norm_b", "k_norm_b",
        "q_norm_c", "k_norm_c", "rel_bias", "w_out"]


def kernel(**inputs):
    import concourse.bacc as bacc
    from concourse.bass_utils import run_bass_kernel_spmd

    nc = bacc.Bacc("TRN2", target_bir_lowering=False, num_devices=1)
    arrays, args = {}, []
    for name in _INS:
        arrays[name] = np.ascontiguousarray(inputs[name])
    arrays["selector"] = bias_selector()
    arrays["rope"] = rope_table()
    arrays["identity"] = np.eye(P, dtype=np.float32)
    for name, a in arrays.items():
        args.append(nc.dram_tensor(name, a.shape, F32, kind="ExternalInput").ap())
    outs = [("y_prompt", (1, SEQS[0], D)), ("y_sample", (1, SEQS[1], D))]
    for name, shape in outs:
        args.append(nc.dram_tensor(name, shape, F32, kind="ExternalOutput").ap())
    build(nc, *args)
    r = run_bass_kernel_spmd(nc, [arrays], core_ids=[0])
    return tuple(r.results[0][name] for name, _ in outs)
```
